# Optimizing a Trainium2 kernel written in Bass

```python
import jax, jax.numpy as jnp
from jax import lax
import numpy as np

D_MODEL = 2048
BATCH = 1
SEQ = 256
DEPTH = 1
DEC_BATCH = 8
DEC_SEQ = 1
PAST_LEN = 256
PAGE_SIZE = 128

RWKV_HEADS = 16
RWKV_HEAD_DIM = 64
D_RWKV = RWKV_HEADS * RWKV_HEAD_DIM
D_DECAY_LORA = 64
D_ICLR_LORA = 64
D_GATE_LORA = 160
D_RWKV_PROJ = 3 * D_RWKV + D_DECAY_LORA + D_ICLR_LORA + D_GATE_LORA
RWKV_LN_EPS = 64e-5

ATT_HEAD_DIM = 64
ATT_GROUPS = ((128, 1), (512, 4), (2048, 16))
HEADS_PER_GROUP = 4
ATT_HEADS = HEADS_PER_GROUP * len(ATT_GROUPS)
D_ATT = ATT_HEADS * ATT_HEAD_DIM
ROPE_THETA = 10000.0

D_FF = 5632

N_IN = D_RWKV_PROJ + 3 * D_ATT + 2 * D_MODEL
NORM_EPS = 1e-6
NEG_INF = -1e30

kernel_name = "hybrid_rwkv7_dilated_attn_macaron_step"

def f32(t):
    return t.astype(jnp.float32)

def rms_norm(x, g):
    xf = f32(x)
    y = xf * lax.rsqrt(jnp.mean(xf * xf, axis=-1, keepdims=True) + NORM_EPS)
    return (y * f32(g)).astype(x.dtype)

def swiglu_half_ffn(x, norm_g, w_in, w_out):
    h = rms_norm(x, norm_g)
    gate, up = jnp.split(h @ w_in, 2, axis=-1)
    return 0.5 * ((jax.nn.silu(gate) * up) @ w_out)

def rotary(x, positions):
    half = x.shape[-1] // 2
    inv_freq = ROPE_THETA ** (-jnp.arange(half, dtype=jnp.float32) / half)
    ang = f32(positions)[:, None] * inv_freq[None, :]
    cos = jnp.cos(ang)[None, :, None, :]
    sin = jnp.sin(ang)[None, :, None, :]
    x1, x2 = jnp.split(f32(x), 2, axis=-1)
    return jnp.concatenate([x1 * cos - x2 * sin, x2 * cos + x1 * sin], axis=-1).astype(x.dtype)

def rwkv7_recurrence(r, w, k, v, kk, a, state0):
    def step(S, inp):
        r_t, w_t, k_t, v_t, kk_t, a_t = inp
        sa = jnp.einsum('bhvk,bhk->bhv', S, -kk_t)
        S = (S * w_t[:, :, None, :] + sa[..., None] * (kk_t * a_t)[:, :, None, :]
             + v_t[..., None] * k_t[:, :, None, :])
        return S, jnp.einsum('bhvk,bhk->bhv', S, r_t)
    xs = tuple(jnp.moveaxis(t, 1, 0) for t in (r, w, k, v, kk, a))
    S, ys = lax.scan(step, state0, xs)
    return jnp.moveaxis(ys, 0, 1), S

def rwkv7_mixer(p, shift_prev, wkv_prev, mu, w0, w2, a0, a2, g2, k_k, k_a, r_k, ln_w, ln_b):
    B, T, _ = p.shape
    pf = f32(p)
    p_prev = jnp.concatenate([f32(shift_prev)[:, None], pf[:, :-1]], axis=1)
    pm = pf + (p_prev - pf) * f32(mu)
    r, k, v, w_low, a_low, g_low = jnp.split(
        pm, [D_RWKV, 2 * D_RWKV, 3 * D_RWKV, 3 * D_RWKV + D_DECAY_LORA,
             3 * D_RWKV + D_DECAY_LORA + D_ICLR_LORA], axis=-1)
    w_log = -jax.nn.softplus(-(f32(w0) + jnp.tanh(w_low) @ f32(w2))) - 0.5
    decay = jnp.exp(-jnp.exp(w_log))
    a = jax.nn.sigmoid(f32(a0) + a_low @ f32(a2))
    g = jax.nn.sigmoid(g_low) @ f32(g2)
    kk = k * f32(k_k)
    k = k * (1.0 + (a - 1.0) * f32(k_a))

    def heads(t):
        return t.reshape(B, T, RWKV_HEADS, RWKV_HEAD_DIM)
    r, k, v, decay, a, kk = map(heads, (r, k, v, decay, a, kk))
    kk = kk / jnp.maximum(jnp.sqrt(jnp.sum(kk * kk, axis=-1, keepdims=True)), 1e-12)
    y, S = rwkv7_recurrence(r, decay, k, v, kk, a, f32(wkv_prev))
    mean = jnp.mean(y, axis=-1, keepdims=True)
    var = jnp.mean(jnp.square(y - mean), axis=-1, keepdims=True)
    yn = ((y - mean) * lax.rsqrt(var + RWKV_LN_EPS)).reshape(B, T, D_RWKV) * f32(ln_w) + f32(ln_b)
    bonus = (jnp.sum(r * k * f32(r_k), axis=-1, keepdims=True) * v).reshape(B, T, D_RWKV)
    out = (yn + bonus) * g
    return out.astype(p.dtype), p[:, -1], S.astype(p.dtype)

def dilated_group_attention(q, k_ctx, v_ctx, n_past, window, dilation):
    T = q.shape[1]
    n_keys = window // dilation + 1
    idx = n_past + jnp.arange(T)[:, None] - dilation * jnp.arange(n_keys)[None, :]
    valid = idx >= 0
    idx = jnp.maximum(idx, 0)
    kg = jnp.take(k_ctx, idx, axis=1)
    vg = jnp.take(v_ctx, idx, axis=1)
    s = f32(jnp.einsum('bthd,btjhd->bthj', q, kg)) * (ATT_HEAD_DIM ** -0.5)
    s = jnp.where(valid[None, :, None, :], s, NEG_INF)
    lse = jax.nn.logsumexp(s, axis=-1)
    p = jnp.exp(s - lse[..., None])
    o = jnp.einsum('bthj,btjhd->bthd', p.astype(v_ctx.dtype), vg)
    return o, lse

def dilated_attention(q, k, v, positions, kv_pasts, q_norm, k_norm):
    B, T = q.shape[:2]
    q = rotary(rms_norm(q, q_norm), positions)
    k = rotary(rms_norm(k, k_norm), positions)
    outs, lses, new_bufs = [], [], []
    for g, (window, dilation) in enumerate(ATT_GROUPS):
        hs = slice(g * HEADS_PER_GROUP, (g + 1) * HEADS_PER_GROUP)
        kv_new = jnp.stack([k[:, :, hs], v[:, :, hs]], axis=2)
        ctx = jnp.concatenate([kv_pasts[g].astype(kv_new.dtype), kv_new], axis=1)
        n_past = kv_pasts[g].shape[1]
        o, lse = dilated_group_attention(q[:, :, hs], ctx[:, :, 0], ctx[:, :, 1], n_past, window, dilation)
        outs.append(o)
        lses.append(lse)
        keep = min(window, ctx.shape[1])
        new_bufs.append(ctx[:, ctx.shape[1] - keep:])
    alpha = jax.nn.softmax(jnp.stack(lses, axis=0), axis=0)
    o = jnp.concatenate([outs[g] * alpha[g][..., None].astype(outs[g].dtype)
                         for g in range(len(ATT_GROUPS))], axis=2)
    return o.reshape(B, T, D_ATT), new_bufs

def hybrid_layer(x, positions, shift_prev, wkv_prev, kv_pasts, params):
    (ffn1_norm, ffn1_w_in, ffn1_w_out, mix_norm, w_in, b_gate,
     rwkv_mu, rwkv_w0, rwkv_w2, rwkv_a0, rwkv_a2, rwkv_g2, rwkv_k_k, rwkv_k_a, rwkv_r_k,
     rwkv_ln_w, rwkv_ln_b, w_branch_rwkv, attn_q_norm, attn_k_norm, w_branch_attn, w_out,
     ffn2_norm, ffn2_w_in, ffn2_w_out) = params
    B, T, _ = x.shape
    x = x + swiglu_half_ffn(x, ffn1_norm, ffn1_w_in, ffn1_w_out)
    h = rms_norm(x, mix_norm)
    proj = h @ w_in
    p_rwkv, p_att, p_gate = jnp.split(proj, [D_RWKV_PROJ, D_RWKV_PROJ + 3 * D_ATT], axis=-1)
    o_a, shift_new, wkv_new = rwkv7_mixer(p_rwkv, shift_prev, wkv_prev, rwkv_mu, rwkv_w0, rwkv_w2,
                                          rwkv_a0, rwkv_a2, rwkv_g2, rwkv_k_k, rwkv_k_a, rwkv_r_k,
                                          rwkv_ln_w, rwkv_ln_b)
    q, k, v = (t.reshape(B, T, ATT_HEADS, ATT_HEAD_DIM) for t in jnp.split(p_att, 3, axis=-1))
    o_b, new_bufs = dilated_attention(q, k, v, positions, kv_pasts, attn_q_norm, attn_k_norm)
    g_a, g_b = jnp.split(jax.nn.sigmoid(p_gate + b_gate), 2, axis=-1)
    merged = g_a * (o_a @ w_branch_rwkv) + g_b * (o_b @ w_branch_attn)
    x = x + merged @ w_out
    x = x + swiglu_half_ffn(x, ffn2_norm, ffn2_w_in, ffn2_w_out)
    return x, shift_new, wkv_new, new_bufs

def setup_inputs(seed: int = 0) -> dict:
    key = jax.random.key(seed)
    nk = iter(jax.random.split(key, 48))

    def normal(shape, scale=1.0):
        return jax.random.normal(next(nk), shape, jnp.float32) * scale

    def gain(shape):
        return 1.0 + normal(shape, 0.1)

    L = DEPTH
    win_lens = [min(w, PAST_LEN) for w, _ in ATT_GROUPS]
    return {
        "x_prompt": normal((BATCH, SEQ, D_MODEL)),
        "x_sample": normal((DEC_BATCH, DEC_SEQ, D_MODEL)),
        "state_rwkv_shift": normal((L, DEC_BATCH, D_RWKV_PROJ)),
        "state_rwkv_wkv": normal((L, DEC_BATCH, RWKV_HEADS, RWKV_HEAD_DIM, RWKV_HEAD_DIM), 0.3),
        "cache_att_w128": normal((L, DEC_BATCH, win_lens[0], 2, HEADS_PER_GROUP, ATT_HEAD_DIM)),
        "cache_att_w512": normal((L, DEC_BATCH, win_lens[1], 2, HEADS_PER_GROUP, ATT_HEAD_DIM)),
        "cache_att_w2048": normal((L, DEC_BATCH, win_lens[2], 2, HEADS_PER_GROUP, ATT_HEAD_DIM)),
        "ffn1_norm": gain((L, D_MODEL)),
        "ffn1_w_in": normal((L, D_MODEL, 2 * D_FF), D_MODEL ** -0.5),
        "ffn1_w_out": normal((L, D_FF, D_MODEL), D_FF ** -0.5),
        "mix_norm": gain((L, D_MODEL)),
        "w_in": normal((L, D_MODEL, N_IN), D_MODEL ** -0.5),
        "b_gate": normal((L, 2 * D_MODEL), 0.1),
        "rwkv_mu": jax.random.uniform(next(nk), (L, D_RWKV_PROJ), jnp.float32, 0.0, 1.0),
        "rwkv_w0": jax.random.uniform(next(nk), (L, D_RWKV), jnp.float32, -6.0, -1.0),
        "rwkv_w2": normal((L, D_DECAY_LORA, D_RWKV), 0.1 * D_DECAY_LORA ** -0.5),
        "rwkv_a0": normal((L, D_RWKV), 0.1),
        "rwkv_a2": normal((L, D_ICLR_LORA, D_RWKV), D_ICLR_LORA ** -0.5),
        "rwkv_g2": normal((L, D_GATE_LORA, D_RWKV), D_GATE_LORA ** -0.5),
        "rwkv_k_k": 0.85 + normal((L, D_RWKV), 0.05),
        "rwkv_k_a": 1.0 + normal((L, D_RWKV), 0.05),
        "rwkv_r_k": normal((L, RWKV_HEADS, RWKV_HEAD_DIM), 0.1),
        "rwkv_ln_w": gain((L, D_RWKV)),
        "rwkv_ln_b": normal((L, D_RWKV), 0.02),
        "w_branch_rwkv": normal((L, D_RWKV, D_MODEL), D_RWKV ** -0.5),
        "attn_q_norm": gain((L, ATT_HEAD_DIM)),
        "attn_k_norm": gain((L, ATT_HEAD_DIM)),
        "w_branch_attn": normal((L, D_ATT, D_MODEL), D_ATT ** -0.5),
        "w_out": normal((L, D_MODEL, D_MODEL), D_MODEL ** -0.5),
        "ffn2_norm": gain((L, D_MODEL)),
        "ffn2_w_in": normal((L, D_MODEL, 2 * D_FF), D_MODEL ** -0.5),
        "ffn2_w_out": normal((L, D_FF, D_MODEL), D_FF ** -0.5),
    }

def reference(x_prompt, x_sample, state_rwkv_shift, state_rwkv_wkv, cache_att_w128, cache_att_w512,
              cache_att_w2048, ffn1_norm, ffn1_w_in, ffn1_w_out, mix_norm, w_in, b_gate, rwkv_mu, rwkv_w0,
              rwkv_w2, rwkv_a0, rwkv_a2, rwkv_g2, rwkv_k_k, rwkv_k_a, rwkv_r_k, rwkv_ln_w, rwkv_ln_b,
              w_branch_rwkv, attn_q_norm, attn_k_norm, w_branch_attn, w_out, ffn2_norm, ffn2_w_in, ffn2_w_out):
    params = (ffn1_norm, ffn1_w_in, ffn1_w_out, mix_norm, w_in, b_gate,
              rwkv_mu, rwkv_w0, rwkv_w2, rwkv_a0, rwkv_a2, rwkv_g2, rwkv_k_k, rwkv_k_a, rwkv_r_k,
              rwkv_ln_w, rwkv_ln_b, w_branch_rwkv, attn_q_norm, attn_k_norm, w_branch_attn, w_out,
              ffn2_norm, ffn2_w_in, ffn2_w_out)
    pos_prompt = jnp.arange(SEQ)
    pos_sample = PAST_LEN + jnp.arange(DEC_SEQ)
    y_p, y_s = x_prompt, x_sample
    p_shift, p_wkv, s_shift, s_wkv = [], [], [], []
    p_kv = [[] for _ in ATT_GROUPS]
    s_kv = [[] for _ in ATT_GROUPS]
    for l in range(DEPTH):
        lp = tuple(w[l] for w in params)
        empty_kv = tuple(jnp.zeros((BATCH, 0, 2, HEADS_PER_GROUP, ATT_HEAD_DIM), x_prompt.dtype)
                         for _ in ATT_GROUPS)
        y_p, sh, wk, bufs = hybrid_layer(
            y_p, pos_prompt, jnp.zeros((BATCH, D_RWKV_PROJ), x_prompt.dtype),
            jnp.zeros((BATCH, RWKV_HEADS, RWKV_HEAD_DIM, RWKV_HEAD_DIM), jnp.float32), empty_kv, lp)
        p_shift.append(sh)
        p_wkv.append(wk)
        for g in range(len(ATT_GROUPS)):
            p_kv[g].append(bufs[g])
        y_s, sh, wk, bufs = hybrid_layer(
            y_s, pos_sample, state_rwkv_shift[l], state_rwkv_wkv[l],
            (cache_att_w128[l], cache_att_w512[l], cache_att_w2048[l]), lp)
        s_shift.append(sh)
        s_wkv.append(wk)
        for g in range(len(ATT_GROUPS)):
            s_kv[g].append(bufs[g])
    return (y_p, y_s,
            jnp.stack(p_shift), jnp.stack(p_wkv),
            jnp.stack(p_kv[0]), jnp.stack(p_kv[1]), jnp.stack(p_kv[2]),
            jnp.stack(s_shift), jnp.stack(s_wkv),
            jnp.stack(s_kv[0]), jnp.stack(s_kv[1]), jnp.stack(s_kv[2]))


_drawn_inputs = setup_inputs


def setup_inputs(seed=0):
    import zlib

    import numpy as np

    out = dict(_drawn_inputs(seed))
    spreads = {}
    factors = {'b_gate': 5.075, 'rwkv_w2': 8.0, 'rwkv_ln_b': 8.0, 'attn_q_norm': 8.0}
    for name, (base, spread) in spreads.items():
        noise = np.random.default_rng([zlib.crc32(name.encode()), seed]).standard_normal(out[name].shape)
        drawn = base * np.exp(spread * noise) if base else spread * noise
        out[name] = __import__('jax').numpy.asarray(drawn.astype(out[name].dtype))
    for name, factor in factors.items():
        out[name] = (out[name] * factor).astype(out[name].dtype)
    return out
```

```python
from contextlib import ExitStack

import numpy as np

import concourse.bass as bass
from concourse import mybir

F32 = mybir.dt.float32
F32R = mybir.dt.float32r
ACT = mybir.ActivationFunctionType
ALU = mybir.AluOpType
AX = mybir.AxisListType

P = 128
SEQ, DEC = 256, 8
T = SEQ + DEC
D = 2048
DT = D // P
D_FF = 5632
FT = D_FF // P
FFN_PARTS = (16, 16, 12)
assert sum(FFN_PARTS) == FT
HEADS, HD = 16, 64
D_RW = HEADS * HD
RT = D_RW // P
PAIRS = HEADS // 2
N_RW = 3 * D_RW + 64 + 64 + 160
A_HEADS, HPG = 12, 4
D_AT = A_HEADS * HD
AT = D_AT // P
GROUPS = ((128, 1), (512, 4), (2048, 16))
PAST = 256
C = 64
NCH = SEQ // C
S_PREP, S_CHUNK = 6, 8
S_LOOP = S_PREP + S_CHUNK * NCH
EPS = 1e-6
LN_EPS = 64e-5
DECAY = float(np.exp(-0.5))
SCALE = HD ** -0.5
LORA0 = 3 * D_RW
G_LAST = N_RW - P

LOOK = 3
RING = 4
BANKS = 4
BODY = 4
HALF = 8 * P
AUX = 4

PHASES = []
for f in (1, 2):
    part = []
    for q, kt in enumerate(FFN_PARTS):
        part += [(f"ffn{f}_in{q}", 2 * kt, DT), (f"ffn{f}_out{q}", DT, kt)]
    PHASES += part if f == 2 else part + [
        ("lora", 3, DT), ("rkv", 3 * RT, DT), ("side", 3 * AT + 2 * DT, DT),
        ("branch", DT, RT + AT), ("out", DT, DT)]
FIRST, KT_OF, OFFSET = {}, [], []
for name, n, kt in PHASES:
    FIRST[name] = len(KT_OF)
    for _ in range(n):
        OFFSET.append(sum(KT_OF[-1:]) + (OFFSET[-1] if OFFSET else 0))
        KT_OF.append(kt)
NBLK = len(KT_OF)
NTILES = OFFSET[-1] + KT_OF[-1]
PHASE = {name: (FIRST[name], n, kt) for name, n, kt in PHASES}


def constants():
    s, t = np.arange(P)[:, None] % C, np.arange(C)[None]
    tok = np.arange(T)
    c = {}
    c["blocks"] = np.kron(np.eye(2), np.ones((HD, HD)))
    c["blocks64"] = c["blocks"] / HD
    c["pairsum"] = c["blocks"][:, ::HD]
    c["ident"] = np.eye(P)
    c["ident64"] = np.tile(np.eye(HD), (2, 1))
    c["causal"] = np.concatenate([s < t, s <= t], 1)
    for lv in range(6):
        b = 1 << lv
        c[f"join{lv}"] = (s // (2 * b) == t // (2 * b)) & (s // b % 2 == 0) & (t // b % 2 == 1)
    c["join0t"] = (s // 2 == t // 2) & (t % 2 == 0) & (s % 2 == 1)
    d = np.arange(P)
    rot = np.zeros((P, P))
    for m in range(P):
        if m % HD < HD // 2:
            rot[m + HD // 2, m] = -1.0
        else:
            rot[m - HD // 2, m] = 1.0
    c["rot"] = rot
    pos = np.where(tok < SEQ, tok, PAST).astype(np.float32)
    freq = (np.float32(10000.0) ** (-np.arange(HD // 2, dtype=np.float32) / np.float32(HD // 2)))[d % (HD // 2)]
    ang = (freq[:, None] * pos[None]).astype(np.float32)
    c["carry"] = np.tile((tok % C != 0) & (tok < SEQ), (P, 1))
    c["cos"], c["sin"] = np.cos(ang), np.sin(ang)
    p = np.arange(P)[:, None]
    mask = []
    for window, step in GROUPS:
        for q0, keys in ((0, P), (P, SEQ)):
            back = q0 + p - np.arange(keys)[None]
            mask.append(np.where((back >= 0) & (back <= window) & (back % step == 0), 0.0, -1e30))
    c["mask"] = np.concatenate(mask, 1)
    return {k: np.asarray(v, np.float32) for k, v in c.items()}


CONST = constants()
CAT, at = {}, 0
for k, v in CONST.items():
    CAT[k] = (at, v.shape[1])
    at += v.shape[1]
MASK0, COS0 = CAT["mask"][0], CAT["cos"][0]
assert MASK0 + CAT["mask"][1] == at

PARAMS = (("mu", 3 * RT + 3), ("w0", RT), ("a0", RT), ("kk", RT), ("ka", RT), ("rk", RT), ("lnw", RT), ("lnb", RT),
          ("bg", 2 * DT), ("qn", 1), ("kn", 1))
PAR, at = {}, 0
for k, n in PARAMS:
    PAR[k] = (at, n)
    at += n
NPAR = at
KEYS = (P, C, C // 4)
KOFF = (0, P, P + C)
NKEYS = sum(KEYS)
KOUT = [min(w, PAST + 1) for w, _ in GROUPS]


def walk(eng, name, body):
    _, n, _ = PHASE[name]
    loops = (n - 2) // BODY
    if loops >= 2:
        with eng.Fori(0, loops) as i:
            for k in range(BODY):
                body(k, i)
    for k in range(BODY * loops if loops >= 2 else 0, n):
        body(k, 0)


def build(nc, ins, outs, side):
    with ExitStack() as ctx:
        def sb(name, shape, dt=F32, where=ctx):
            return where.enter_context(nc.sbuf_tensor(name, shape, dt))

        def sem(name):
            return ctx.enter_context(nc.semaphore(name))

        raw = sb("raw", [P, RING, HALF])
        whi = sb("whi", [P, RING, HALF], F32R)
        wlo = sb("wlo", [P, RING, HALF], F32R)
        x = sb("x", [P, DT, T])
        xin_gains = sb("gains", [P, 3, DT])
        ones = sb("ones", [P, P])
        rstd = sb("rstd", [P, T])
        eps = sb("eps", [P, 2])
        banks = [ctx.enter_context(nc.psum_tensor(f"bank{i}", [P, 512], F32)) for i in range(8)]
        hhi = sb("hhi", [P, DT, T], F32R)
        hlo = sb("hlo", [P, DT, T], F32R)

        with ExitStack() as ffn:
            mhi = sb("mhi", [P, max(FFN_PARTS), T], F32R, ffn)
            mlo = sb("mlo", [P, max(FFN_PARTS), T], F32R, ffn)
            silu = sb("silu", [P, 2, T], F32, ffn)
            prod = sb("prod", [P, 2, T], F32, ffn)
            sq = sb("sq", [P, 2, 4, T], F32, ffn)
            ht = sb("ht", [P, 4, T], F32, ffn)

        loaded = sem("loaded")
        x_in = [sem(f"x_in{q}") for q in range(4)]
        landed = [sem(f"landed{r}") for r in range(RING)]
        hi_done = sem("hi_done")
        lo_done = sem("lo_done")
        half_done = sem("half_done")
        evac = sem("evac")
        silu_done = sem("silu_done")
        mid_done = sem("mid_done")
        sq_done, sq_used, ss_done, root_done, h_done = map(
            sem, ("sq_done", "sq_used", "ss_done", "root_done", "h_done"))
        stored = sem("stored")

        act, dve, pe = nc.scalar, nc.vector, nc.tensor
        w = ins["weights"]

        def split_hi(u, i, n):
            act.wait_ge(landed[u % RING], 16 * (u // RING + 1) + 16 * (2 * BODY // RING) * i)
            if u >= RING or not isinstance(i, int):
                act.wait_ge(half_done, u - RING + 2 + 2 * BODY * i)
            act.activation(whi[:, u % RING, 0:n], raw[:, u % RING, 0:n], ACT.Copy).then_inc(hi_done, 1)

        def split_lo(u, i, n):
            s = u % RING
            dve.wait_ge(hi_done, u + 1 + 2 * BODY * i)
            dve.tensor_tensor(wlo[:, s, 0:n], raw[:, s, 0:n], whi[:, s, 0:n].bitcast(F32),
                              ALU.subtract).then_inc(lo_done, 1)

        def ahead(name, n, i, split):
            for half in range(2):
                u = 2 * (FIRST[name] + n) + half + LOOK
                if u < 2 * NBLK:
                    split(u, i, KT_OF[u // 2] // 2 * P)

        def products(name, n, i, parts, before=None, halves=(0, 1)):
            b = FIRST[name] + n
            tiles = [(bank, k, kt, xhi, xlo) for bank, kt, xhi, xlo in parts for k in range(kt)]
            assert len(tiles) == KT_OF[b]
            if 0 in halves:
                pe.wait_ge(evac, b + 1 + BODY * i)
            for half in halves:
                u = 2 * b + half
                pe.wait_ge(lo_done, u + 1 + 2 * BODY * i)
                h = len(tiles) // 2
                for c in range(h):
                    bank, k, kt, xhi, xlo = tiles[half * h + c]
                    if before is not None:
                        before(half * h + c)
                    hi, lo = (t[:, u % RING, c * P:(c + 1) * P] for t in (whi, wlo))
                    pe.matmul(bank[:, 0:T], hi, xhi[:, k], start=(k == 0), stop=False)
                    pe.matmul(bank[:, 0:T], hi, xlo[:, k], start=False, stop=False)
                    mm = pe.matmul(bank[:, 0:T], lo, xhi[:, k], start=False, stop=(k == kt - 1))
                mm.then_inc(half_done, 1)

        def block_done(eng, name, n, i):
            eng.wait_ge(half_done, 2 * (FIRST[name] + n) + 3 + 2 * BODY * i)

        def result(name, n):
            return banks[(FIRST[name] + n) % BANKS]

        NORMS = 3
        last_out = [f"ffn1_out{len(FFN_PARTS) - 1}", "out"]

        def x_ready(eng, r, q):
            if r == 0:
                eng.wait_ge(x_in[q], 16)
            else:
                name = last_out[r - 1]
                eng.wait_ge(evac, BANKS + FIRST[name] + 4 * q + 4)

        def norm_act(r):
            for q in range(4):
                x_ready(act, r, q)
                u = 4 * r + q
                if u >= 2:
                    act.wait_ge(sq_used, u - 1)
                act.activation(sq[:, q % 2], x[:, 4 * q:4 * q + 4], ACT.Square).then_inc(sq_done, 1)
            if r == 0:
                split_hi(0, 0, HALF)
                act.wait_ge(evac, BANKS)
            act.wait_ge(ss_done, r + 1)
            act.activation(rstd[:], banks[7][:, 0:T], ACT.Sqrt, scale=1.0 / D, bias=eps[:, 0:1]).then_inc(root_done, 1)

        def norm_pe(r):
            for q in range(4):
                pe.wait_ge(sq_done, 4 * r + q + 1)
                for k in range(4):
                    mm = pe.matmul(banks[7][:, 0:T], ones[:], sq[:, q % 2, k], start=(q == 0 and k == 0),
                                   stop=(q == 3 and k == 3))
                mm.then_inc(sq_used, 1)
            pe.wait_ge(sq_used, 4 * r + 4)
            pe.sem_inc(ss_done, 1)

        def norm_dve(r):
            for q in range(4):
                x_ready(dve, r, q)
            if r == 0:
                dve.wait_ge(loaded, LOADED)
            dve.wait_ge(root_done, r + 1)
            dve.reciprocal(rstd[:], rstd[:])
            for q in range(4):
                dve.drain()
                for k in range(4):
                    n = 4 * q + k
                    dve.scalar_tensor_tensor(ht[:, k], x[:, n], xin_gains[:, r, n:n + 1], rstd[:], ALU.mult, ALU.mult)
                dve.drain()
                dve.tensor_copy(hhi[:, 4 * q:4 * q + 4], ht[:])
                dve.drain()
                dve.tensor_tensor(hlo[:, 4 * q:4 * q + 4], ht[:], hhi[:, 4 * q:4 * q + 4].bitcast(F32),
                                  ALU.subtract).then_inc(h_done, 4)

        def ffn_pe(f, r):
            for q, kt in enumerate(FFN_PARTS):
                def h_there(k):
                    if k % 4 == 0:
                        pe.wait_ge(h_done, DT * r + k + 4)
                pairs = (FT if f == 2 else 0) + sum(FFN_PARTS[:q])

                def hidden_there(k):
                    if k == 0 or k >= kt - 2:
                        pe.wait_ge(mid_done, pairs + max(k + 1, kt - 2))
                walk(pe, f"ffn{f}_in{q}", lambda n, i: products(
                    f"ffn{f}_in{q}", n, i, [(result(f"ffn{f}_in{q}", n), DT, hhi, hlo)],
                    h_there if n == 0 and q == 0 else None))
                walk(pe, f"ffn{f}_out{q}", lambda n, i: products(
                    f"ffn{f}_out{q}", n, i, [(result(f"ffn{f}_out{q}", n), kt, mhi, mlo)],
                    hidden_there if n == 0 else None))

        def ffn_act(f):
            for q in range(len(FFN_PARTS)):
                name = f"ffn{f}_in{q}"

                def gate(n, i):
                    ahead(name, n, i, split_hi)
                    if n % 2 == 0:
                        b = FIRST[name] + n
                        block_done(act, name, n, i)
                        act.wait_ge(evac, b + 2 + BODY * i)
                        act.activation(silu[:, n // 2 % 2], result(name, n)[:, 0:T], ACT.Silu).then_inc(silu_done, 1)
                walk(act, name, gate)
                walk(act, f"ffn{f}_out{q}", lambda n, i: ahead(f"ffn{f}_out{q}", n, i, split_hi))

        def ffn_dve(f):
            for q in range(len(FFN_PARTS)):
                name, out = f"ffn{f}_in{q}", f"ffn{f}_out{q}"
                pairs = (FT if f == 2 else 0) + sum(FFN_PARTS[:q])

                def hidden(n, i):
                    ahead(name, n, i, split_lo)
                    if n % 2 == 1:
                        j, slot = n // 2, n // 2 % 2
                        m = j + 2 * i
                        block_done(dve, name, n, i)
                        dve.wait_ge(silu_done, pairs + j + 1 + 2 * i)
                        dve.tensor_tensor(prod[:, slot], silu[:, slot], result(name, n)[:, 0:T], ALU.mult).then_inc(evac, 1)
                        dve.drain()
                        dve.tensor_copy(mhi[:, m], prod[:, slot]).then_inc(evac, 1)
                        dve.drain()
                        dve.tensor_tensor(mlo[:, m], prod[:, slot], mhi[:, m].bitcast(F32), ALU.subtract).then_inc(mid_done, 1)

                def add(n, i):
                    ahead(out, n, i, split_lo)
                    block_done(dve, out, n, i)
                    m = n + BODY * i
                    dve.scalar_tensor_tensor(x[:, m], result(out, n)[:, 0:T], 0.5, x[:, m], ALU.mult,
                                             ALU.add).then_inc(evac, 1)
                walk(dve, name, hidden)
                walk(dve, out, add)

        LOADED = 16 * 2
        with ExitStack() as mix:
            cst = sb("cst", [P, COS0], F32, mix)
            par = sb("par", [P, NPAR], F32, mix)
            stg = sb("stg", [P, 2, T], F32, mix)
            with ExitStack() as rec:
                rkv = sb("rkv", [P, 3 * RT, T], F32, rec)
                lora = sb("lora", [P, 3, T], F32, rec)
                iclr = sb("iclr", [P, RT, T], F32, rec)
                kkey = sb("kkey", [P, RT, T], F32, rec)
                cum = sb("cum", [P, RT, T], F32, rec)
                cumx = sb("cumx", [P, RT, T], F32, rec)
                nmu = sb("nmu", [P, 3 * RT + 3], F32, rec)
                nka = sb("nka", [P, RT], F32, rec)
                shiftt = sb("shiftt", [P, 3 * RT + 3, DEC], F32, rec)
                last = sb("last", [P, 3 * RT + 3, DEC + 1], F32, rec)
                with ExitStack() as sub:
                    w2a2 = sb("w2a2", [P, D_RW], F32, sub)
                    nrm = sb("nrm", [P, RT, T], F32, sub)
                with ExitStack() as sub:
                    mat = lambda name, w=C: sb(name, [P, PAIRS, w], F32, sub)
                    ar, bc, kc, vc = mat("ar", 2 * C), mat("bc"), mat("kc"), mat("vc")
                    px, pc, pi = mat("px"), mat("pc"), mat("pi")
                    vt, bt, kt_ = mat("vt"), mat("bt"), mat("kt")
                    ab, ak = mat("ab", 2 * C), mat("ak", 2 * C)
                    tm, qm, state = mat("tm"), mat("qm"), mat("state")
                    m1, zm, w1, um = vc, px, pi, pc
                    pend = sb("pend", [P, PAIRS], F32, sub)
                with ExitStack() as sub:
                    g2a = sb("g2a", [P, D_RW], F32, sub)
                    g2b = sb("g2b", [P, D_RW], F32, sub)
                    gn = sb("gn", [P, RT, T], F32, sub)
                    sst = sb("sst", [P, PAIRS, DEC, HD], F32, sub)
                    st = sb("st", [P, DEC, HD], F32, sub)
                    wdec = sb("wdec", [P, PAIRS, DEC], F32, sub)
                    nkk = sb("nkk", [P, PAIRS, DEC], F32, sub)
            oah = sb("oah", [P, RT, T], F32R, mix)
            oal = sb("oal", [P, RT, T], F32R, mix)
            obh = sb("obh", [P, AT, T], F32R, mix)
            obl = sb("obl", [P, AT, T], F32R, mix)
            with ExitStack() as sub:
                qkv = sb("qkv", [P, 3 * AT, T], F32, sub)
                ob = sb("ob", [P, AT, T], F32, sub)
                kvs = qkv[0:DEC, 0:AT, 0:SEQ]
                cossin = sb("cossin", [P, 2, T], F32, sub)
                with ExitStack() as s2:
                    qn2 = sb("qn2", [P, 2 * AT, T], F32, s2)
                with ExitStack() as s2:
                    amask = sb("amask", [P, 3, P + SEQ], F32, s2)
                    vtok = sb("vtok", [P, 2, D_AT], F32, s2)
                    sc = sb("sc", [P, 3, P + SEQ], F32, s2)
                    pt = sb("pt", [P, 3, P + SEQ], F32, s2)
                    mx = sb("mx", [P, 2], F32, s2)
                    nmx = sb("nmx", [P, 2], F32, s2)
                    ls = sb("ls", [P, 2], F32, s2)
                    rl = sb("rl", [P, 2], F32, s2)
                with ExitStack() as s2:
                    kca = sb("kca", [P, DEC, 2 * NKEYS], F32, s2)
                    vca = sb("vca", [P, 2, DEC // 2, 3, HPG * HD], F32, s2)
                    sct = sb("sct", [P, 3, HPG, DEC], F32, s2)
                    pts = sb("pts", [P, 3, HPG, DEC], F32, s2)
                    pnew = sb("pnew", [P, AT, DEC], F32, s2)
                    ss = sb("ss", [DEC, HPG, NKEYS + 3], F32, s2)
                    smx = sb("smx", [DEC, HPG], F32, s2)
            with ExitStack() as sub:
                gates = sb("gates", [P, 2 * DT, T], F32, sub)
                mg = sb("mg", [P, 2, T], F32, sub)

        def cc(name, lo=0, n=None):
            at, width = CAT[name]
            return cst[:, at + lo:at + (width if n is None else lo + n)]

        def bcast(ap2, n):
            return ap2.unsqueeze(2).to_broadcast([P, ap2.shape[1], n])

        def over(ap2, a):
            return ap2.unsqueeze(1).to_broadcast([P, a, ap2.shape[1]])

        def pp(name, j=0, n=None):
            at, width = PAR[name]
            return par[:, at + j:at + (width if n is None else j + n)]

        R_, K_, V_ = rkv[:, 0:RT], rkv[:, RT:2 * RT], rkv[:, 2 * RT:3 * RT]
        A4 = banks[AUX:AUX + 4]

        mix_in = sem("mix_in")
        late_in = sem("late_in")
        amask_in, cache_in = sem("amask_in"), sem("cache_in")
        mixst, kvcopy = sem("mixst"), sem("kvcopy")
        pre_done = sem("pre_done")
        shift_a, shift_v = sem("shift_a"), sem("shift_v")
        lora_act, lora_pe, lora_out, cum_done = sem("lora_act"), sem("lora_pe"), sem("lora_out"), sem("cum_done")
        kk_sq, kk_ss, kk_root, prep = sem("kk_sq"), sem("kk_ss"), sem("kk_root"), sem("prep")
        c_exp, c_op, c_vec = sem("c_exp"), sem("c_op"), sem("c_vec")
        c_pe, c_act, c_free = sem("c_pe"), sem("c_act"), sem("c_free")
        s_pe, s_vec, s_w = sem("s_pe"), sem("s_vec"), sem("s_w")
        n_pe, n_act, n_vec = sem("n_pe"), sem("n_act"), sem("n_vec")
        oa_done, ob_done = sem("oa_done"), sem("ob_done")
        a_pe, a_act, a_vec = sem("a_pe"), sem("a_act"), sem("a_vec")
        t_pe, t_act, t_vec = sem("t_pe"), sem("t_act"), sem("t_vec")
        u_pe, u_act, u_vec = sem("u_pe"), sem("u_act"), sem("u_vec")
        m_done = sem("m_done")

        stg_full, stg_free, spilled = sem("stg_full"), sem("stg_free"), sem("spilled")
        qkv_in, gates_in, gate_done = sem("qkv_in"), sem("gates_in"), sem("gate_done")

        def side_pe(n, i=0, halves=(0, 1)):
            products("side", n, i, [(result("side", n), DT, hhi, hlo)], halves=halves)

        def side_act(n, i=0):
            ahead("side", n, i, split_hi)
            block_done(act, "side", n, i)
            act.wait_ge(stg_free, n + 1 + BODY * i)
            act.activation(stg[:, n % 2], result("side", n)[:, 0:T], ACT.Copy).then_inc(stg_full, 1)
            act.wait_ge(stg_full, n + 1 + BODY * i)
            act.sem_inc(evac, 1)

        def side_dve(n, i=0):
            ahead("side", n, i, split_lo)

        def half(p):
            return slice(HD * p, HD * p + HD)

        def each_head():
            return [(j, p) for j in range(PAIRS) for p in range(2)]

        def mix_pool(gp):
            def spill(m0, m1_):
                with gp.Fori(0, (m1_ - m0) // 2) as i:
                    for k in range(2):
                        gp.wait_ge(stg_full, m0 + k + 1 + 2 * i)
                        gp.dma_start(side[m0 + k + 2 * i], stg[:, (m0 + k) % 2]).then_inc(spilled, 16)
                        gp.wait_ge(spilled, 16 * (m0 + k + 1) + 32 * i)
                        gp.sem_inc(stg_free, 1)

            gp.wait_ge(h_done, DT)
            for g in range(3):
                if g:
                    gp.wait_ge(mid_done, sum(FFN_PARTS[:g]))
                rows = ins[f"cache{g}"].shape[1]
                keep = KOUT[g] - 1
                gp.dma_start(outs[f"skv{g}"][:, 0:keep], ins[f"cache{g}"][:, rows - keep:rows]).then_inc(kvcopy, 16)
            gp.wait_ge(h_done, 2 * DT)
            gp.dma_start(cst[:], ins["consts"][:, 0:COS0]).then_inc(mix_in, 16)
            gp.dma_start(par[:], ins["params"]).then_inc(mix_in, 16)
            gp.dma_start(shiftt[:], ins["shift"]).then_inc(mix_in, 16)
            gp.dma_start(w2a2[:], ins["w2a2"]).then_inc(mix_in, 16)
            gp.sem_inc(stg_free, 2)
            spill(0, S_LOOP + 2)
            gp.wait_ge(c_free, 1 + NCH)
            gp.dma_start(outs["pwkv"], state[:]).then_inc(mixst, 16)
            gp.wait_ge(mixst, 16)
            gp.dma_start(g2a[:], ins["g2a"]).then_inc(late_in, 16)
            gp.dma_start(g2b[:], ins["g2b"]).then_inc(late_in, 16)
            gp.dma_start(sst[:], ins["swkv"]).then_inc(late_in, 16)
            gp.dma_start(outs["last"], last[:]).then_inc(mixst, 16)
            spill(S_LOOP + 2, S_LOOP + 4)
            gp.wait_ge(s_vec, PAIRS)
            gp.dma_start(outs["swkv"], sst[:]).then_inc(mixst, 16)
            spill(S_LOOP + 4, S_LOOP + 8)
            gp.wait_ge(oa_done, 1)
            gp.dma_start(cossin[:], ins["consts"][:, COS0:MASK0].rearrange("p (g n) -> p g n", g=2)).then_inc(qkv_in, 16)
            gp.dma_start(qkv[:], side[0:3 * AT].rearrange("t p n -> p t n")).then_inc(qkv_in, 16)
            spill(S_LOOP + 8, S_LOOP + 10)
            gp.wait_ge(a_vec, 3)
            gp.dma_start(amask[:], ins["consts"][:, MASK0:].rearrange("p (g n) -> p g n", g=3)).then_inc(amask_in, 16)
            gp.dma_start(outs["pkv"], qkv[:, AT:3 * AT, 0:SEQ]).then_inc(mixst, 16)
            spill(S_LOOP + 10, S_LOOP + 12)
            gp.wait_ge(t_act, 1 + 3 * HPG)
            gp.wait_ge(t_vec, 4 * HPG)
            gp.wait_ge(t_pe, 1 + 4 * HPG)
            gp.dma_start(kca[:], ins["kcache"]).then_inc(cache_in, 16)
            for g in range(3):
                gp.dma_start(vca[0:KEYS[g], :, :, g], ins[f"vcache{g}"]).then_inc(cache_in, 16)
            gp.wait_ge(u_act, 1)
            for g in range(3):
                gp.dma_start(outs[f"skv{g}"][:, KOUT[g] - 1].rearrange("b (s f) -> b s f", s=2),
                             kvs[:, g::3]).then_inc(mixst, 16)
            gp.wait_ge(ob_done, 1)
            gp.dma_start(gates[:], side[3 * AT:].rearrange("t p n -> p t n")).then_inc(gates_in, 16)
            gp.wait_ge(mixst, 16 * 7)
            gp.wait_ge(kvcopy, 16 * 3)

        def shift_act(name, dst, mu0):
            def f(n, i):
                ahead(name, n, i, split_hi)
                block_done(act, name, n, i)
                m = n + BODY * i
                act.activation(dst[:, m], result(name, n)[:, 0:T], ACT.Copy,
                               scale=nmu[:, bass.ds(mu0 + m, 1)]).then_inc(shift_a, 1)
            walk(act, name, f)

        def mix_act():
            act.wait_ge(pre_done, 1)
            shift_act("lora", lora, 3 * RT)
            act.wait_ge(shift_v, 3)
            act.activation(lora[0:HD, 0], lora[0:HD, 0], ACT.Tanh)
            act.activation(lora[:, 1:3], lora[:, 1:3], ACT.Sigmoid).then_inc(lora_act, 1)
            for n in range(RT):
                act.wait_ge(lora_pe, 2 * n + 1)
                act.activation(cumx[:, n], A4[2 * n % 4][:, 0:T], ACT.Sigmoid, bias=pp("w0", n, 1)).then_inc(lora_out, 1)
                act.wait_ge(lora_pe, 2 * n + 2)
                act.activation(iclr[:, n], A4[(2 * n + 1) % 4][:, 0:T], ACT.Sigmoid, bias=pp("a0", n, 1)).then_inc(lora_out, 1)
            shift_act("rkv", rkv, 0)
            side_act(0)
            side_act(1)
            for n in range(RT):
                act.wait_ge(kk_ss, n + 1)
                act.activation(nrm[:, n], A4[n % 4][:, 0:T], ACT.Sqrt).then_inc(kk_root, 1)
            for n in range(2, S_PREP):
                side_act(n)
            act.wait_ge(prep, 1)
            with act.Fori(0, NCH) as c:
                extra = lambda k: side_act(S_PREP + k, S_CHUNK // BODY * c)
                cols = bass.ds(c * C, C)
                act.wait_ge(c_free, c + 1)
                act.activation(px[:], cumx[:, :, cols], ACT.Exp, scale=-DECAY)
                act.activation(pc[:], cum[:, :, cols], ACT.Exp, scale=-DECAY)
                act.activation(pi[:], cum[:, :, cols], ACT.Exp, scale=DECAY).then_inc(c_exp, 1)
                act.activation(vc[:], V_[:, :, cols], ACT.Copy).then_inc(c_op, 1)
                extra(0)
                act.wait_ge(c_pe, 9 * c + 3)
                for dst, bank in ((vt, 1), (bt, 2), (kt_, 3)):
                    act.activation(dst[:], A4[bank][:].rearrange("p (j n) -> p j n", n=C), ACT.Copy).then_inc(c_act, 1)
                extra(1)
                for lv in range(1, 6):
                    act.wait_ge(c_m1, 5 * c + lv)
                    act.activation(m1[:], A4[0][:].rearrange("p (j n) -> p j n", n=C), ACT.Copy).then_inc(c_act, 1)
                    extra(1 + lv)
                act.wait_ge(c_w1, 2 * c + 1)
                act.activation(w1[:], A4[3][:].rearrange("p (j n) -> p j n", n=C), ACT.Copy).then_inc(c_act, 1)
                act.wait_ge(c_w1, 2 * c + 2)
                act.activation(um[:], A4[0][:].rearrange("p (j n) -> p j n", n=C), ACT.Copy).then_inc(c_act, 1)
                extra(7)
            side_act(S_LOOP)
            side_act(S_LOOP + 1)
            act.wait_ge(late_in, 48)
            act.activation(wdec[:], cum[:, :, SEQ:T], ACT.Exp, scale=-DECAY).then_inc(s_w, 1)
            side_act(S_LOOP + 2)
            for n in range(RT):
                act.wait_ge(n_vec, n + 1)
                act.activation(gn[:, n], kkey[:, n], ACT.Square).then_inc(n_act, 1)
            side_act(S_LOOP + 3)
            for n in range(RT):
                act.wait_ge(n_pe, RT + n + 1)
                act.activation(gn[:, n], A4[n % 4][:, 0:T], ACT.Sqrt, bias=eps[:, 1:2]).then_inc(n_act, 1)
            for n in range(4, 8):
                side_act(S_LOOP + n)
            act.wait_ge(qkv_in, 32)
            act.activation(qn2[:], qkv[:, 0:2 * AT], ACT.Square).then_inc(a_act, 1)
            for n in range(2 * AT):
                act.wait_ge(a_pe, n + 1)
                act.activation(qn2[:, n], A4[n % 4][:, 0:T], ACT.Sqrt, scale=1.0 / HD, bias=eps[:, 0:1]).then_inc(a_act, 1)
            side_act(S_LOOP + 8)
            side_act(S_LOOP + 9)
            act.wait_ge(a_vec, 3)
            act.wait_ge(t_pe, 1)
            for q in range(2):
                act.activation(vtok[:, q, 0:512], A4[2 * q][:, :], ACT.Copy)
                ins_ = act.activation(vtok[:, q, 512:D_AT], A4[2 * q + 1][:, 0:D_AT - 512], ACT.Copy)
            ins_.then_inc(t_act, 1)
            for hh in range(HPG):
                act.wait_ge(t_vec, 4 * hh + 2)
                act.activation(sc[:, :, 0:P], sc[:, :, 0:P], ACT.Exp, bias=nmx[:, 0:1], accum_out=ls[:, 0:1])
                act.activation(sc[:, :, P:], sc[:, :, P:], ACT.Exp, bias=nmx[:, 1:2], accum_out=ls[:, 1:2])
                act.drain()
                act.sem_inc(t_act, 1)
                if hh < 2:
                    side_act(S_LOOP + 10 + hh)
                act.wait_ge(t_pe, 1 + 4 * hh + 2)
                for g in range(3):
                    ins_ = act.activation(pt[:, g], A4[g][:, 0:P + SEQ], ACT.Copy)
                ins_.then_inc(t_act, 1)
                act.wait_ge(t_pe, 1 + 4 * hh + 4)
                for g in range(3):
                    j, p = divmod(g * HPG + hh, 2)
                    bank, col = ((3, 0), (3, SEQ), (0, 0))[g]
                    ins_ = act.activation(ob[half(p), j, 0:SEQ], A4[bank][half(p), col:col + SEQ], ACT.Copy)
                ins_.then_inc(t_act, 1)
            act.wait_ge(u_pe, 1)
            for q in range(3):
                ins_ = act.activation(kvs[:, 2 * q:2 * q + 2], A4[q][0:DEC, :].rearrange("b (t p) -> b t p", p=SEQ), ACT.Copy)
            ins_.then_inc(u_act, 1)
            act.wait_ge(u_pe, 2)
            for g in range(3):
                nk = KEYS[g]
                for p in range(2):
                    ins_ = act.activation(sct[0:nk, g, p::2],
                                          A4[3 - p][0:nk, g * 32:g * 32 + 32].rearrange("p (h b) -> p h b", b=DEC)[:, p::2],
                                          ACT.Copy, scale=SCALE)
            ins_.then_inc(u_act, 1)
            act.wait_ge(u_pe, 3)
            for q in range(2):
                act.activation(ss[:, 2 * q:2 * q + 2, 0:NKEYS],
                               A4[1 + q][0:DEC, 0:2 * NKEYS].rearrange("b (h n) -> b h n", n=NKEYS), ACT.Copy)
            act.activation(ss[:, :, NKEYS:], A4[0][0:DEC, 0:A_HEADS].rearrange("b (g h) -> b h g", h=HPG),
                           ACT.Copy, scale=SCALE).then_inc(u_act, 1)
            act.wait_ge(u_vec, 2)
            act.activation(ss[:], ss[:], ACT.Exp).then_inc(u_act, 1)
            act.wait_ge(u_pe, 4)
            for g in range(3):
                nk = KEYS[g]
                act.activation(pts[0:nk, g], A4[3][0:nk, g * 32:g * 32 + 32].rearrange("p (h b) -> p h b", b=DEC), ACT.Copy)
            act.activation(pnew[:], A4[1][:, 0:AT * DEC].rearrange("p (t b) -> p t b", b=DEC), ACT.Copy).then_inc(u_act, 1)
            act.wait_ge(gates_in, 16)

            def gate(n, i):
                ahead("branch", n, i, split_hi)
                for q in range(2):
                    m = q * DT + n + BODY * i
                    act.activation(gates[:, m], gates[:, m], ACT.Sigmoid,
                                   bias=par[:, bass.ds(PAR["bg"][0] + m, 1)]).then_inc(gate_done, 1)
            walk(act, "branch", gate)
            walk(act, "out", lambda n, i: ahead("out", n, i, split_hi))

        def shift_dve(name, dst, mu0):
            def f(n, i):
                ahead(name, n, i, split_lo)
                k = n + BODY * i
                dve.wait_ge(shift_a, (3 if name == "rkv" else 0) + n + 1 + BODY * i)
                m = mu0 + k
                mu, res = par[:, bass.ds(m, 1)], result(name, n)
                dve.scalar_tensor_tensor(dst[:, k, 1:SEQ], res[:, 0:SEQ - 1], mu, dst[:, k, 1:SEQ], ALU.mult, ALU.add)
                dve.scalar_tensor_tensor(dst[:, k, SEQ:T], shiftt[:, m], mu, dst[:, k, SEQ:T], ALU.mult,
                                         ALU.add).then_inc(shift_v, 1)
                dve.tensor_copy(last[:, m], res[:, SEQ - 1:T]).then_inc(evac, 1)
            walk(dve, name, f)

        def mix_dve():
            dve.wait_ge(mix_in, 64)
            dve.tensor_scalar(nmu[:], pp("mu"), -1.0, 1.0, ALU.mult, ALU.add)
            dve.tensor_scalar(nka[:], pp("ka"), -1.0, 1.0, ALU.mult, ALU.add)
            dve.drain()
            dve.sem_inc(pre_done, 1)
            shift_dve("lora", lora, 3 * RT)
            dve.wait_ge(lora_out, 2 * RT)
            for n in range(RT):
                dve.tensor_tensor_scan(cum[:, n], cc("carry"), cumx[:, n], 0.0, ALU.mult, ALU.add)
            dve.drain()
            dve.tensor_tensor(cumx[:], cum[:], cumx[:], ALU.subtract)
            shift_dve("rkv", rkv, 0)
            dve.drain()
            dve.tensor_tensor(kkey[:], K_, bcast(pp("kk"), T), ALU.mult)
            dve.drain()
            dve.tensor_tensor(nrm[:], kkey[:], kkey[:], ALU.mult).then_inc(kk_sq, 1)
            side_dve(0)
            side_dve(1)
            dve.wait_ge(kk_root, RT)
            dve.tensor_scalar(nrm[:], nrm[:], 1e-12, None, ALU.max)
            dve.drain()
            dve.reciprocal(nrm[:], nrm[:])
            dve.drain()
            dve.tensor_tensor(kkey[:], kkey[:], nrm[:], ALU.mult)
            side_dve(2)
            dve.drain()
            dve.tensor_tensor(nrm[:], iclr[:], bcast(pp("ka"), T), ALU.mult)
            dve.tensor_tensor(iclr[:], iclr[:], kkey[:], ALU.mult)
            side_dve(3)
            dve.drain()
            dve.tensor_tensor(nrm[:], nrm[:], bcast(nka[:], T), ALU.add)
            dve.drain()
            dve.tensor_tensor(K_, K_, nrm[:], ALU.mult)
            side_dve(4)
            dve.drain()
            dve.memset(state[:], 0.0)
            dve.drain()
            dve.sem_inc(prep, 1)
            dve.sem_inc(c_free, 1)
            side_dve(5)
            with dve.Fori(0, NCH) as c:
                extra = lambda k: side_dve(S_PREP + k, S_CHUNK // BODY * c)
                cols = bass.ds(c * C, C)
                dve.wait_ge(c_exp, c + 1)
                dve.scalar_tensor_tensor(ar[:, :, 0:C], kkey[:, :, cols], -1.0, px[:], ALU.mult, ALU.mult)
                dve.tensor_tensor(ar[:, :, C:], R_[:, :, cols], pc[:], ALU.mult)
                dve.tensor_tensor(bc[:], iclr[:, :, cols], pi[:], ALU.mult)
                dve.tensor_tensor(kc[:], K_[:, :, cols], pi[:], ALU.mult)
                dve.tensor_copy(pend[:], pc[:, :, C - 1])
                dve.drain()
                dve.sem_inc(c_vec, 1)
                dve.wait_ge(c_pe, 9 * c + 1)
                for q in range(2):
                    dve.tensor_tensor(ab[:, 4 * q:4 * q + 4], A4[q][:].rearrange("p (j n) -> p j n", n=2 * C),
                                      over(cc("causal"), 4), ALU.mult)
                dve.drain()
                dve.sem_inc(c_vec, 1)
                dve.wait_ge(c_pe, 9 * c + 2)
                for q in range(2):
                    dve.tensor_tensor(ak[:, 4 * q:4 * q + 4], A4[2 + q][:].rearrange("p (j n) -> p j n", n=2 * C),
                                      over(cc("causal"), 4), ALU.mult)
                dve.drain()
                dve.sem_inc(c_vec, 1)
                dve.tensor_tensor(qm[:], ab[:, :, 0:C], over(cc("join0"), PAIRS), ALU.mult)
                extra(0)
                dve.wait_ge(c_pe, 9 * c + 3)
                dve.tensor_tensor(tm[:], A4[0][:].rearrange("p (j n) -> p j n", n=C), over(cc("join0t"), PAIRS), ALU.mult)
                dve.drain()
                dve.tensor_tensor(qm[:], qm[:], over(cc("ident64"), PAIRS), ALU.add)
                dve.tensor_tensor(tm[:], tm[:], over(cc("ident64"), PAIRS), ALU.add)
                for lv in range(1, 6):
                    dve.tensor_tensor(zm[:], ab[:, :, 0:C], over(cc(f"join{lv}"), PAIRS), ALU.mult)
                    dve.drain()
                    dve.sem_inc(c_lv, 1)
                    if lv == 1:
                        extra(1)
                    extra(1 + lv)
                    dve.wait_ge(c_pe, 9 * c + 3 + lv)
                    dve.tensor_tensor(qm[:], qm[:], A4[1][:].rearrange("p (j n) -> p j n", n=C), ALU.add)
                    if lv < 5:
                        dve.tensor_tensor(tm[:], tm[:], A4[2][:].rearrange("p (j n) -> p j n", n=C), ALU.add)
                dve.drain()
                dve.sem_inc(c_lv, 1)
                extra(7)
                dve.wait_ge(c_pe, 9 * c + 9)
                dve.tensor_tensor(state[:], state[:], A4[2][:].rearrange("p (j n) -> p j n", n=C), ALU.add)
                dve.tensor_copy(kkey[:, :, cols], A4[1][:].rearrange("p (j n) -> p j n", n=C))
                dve.drain()
                dve.tensor_tensor(state[:], state[:], bcast(pend[:], C), ALU.mult)
                dve.drain()
                dve.sem_inc(c_free, 1)
            side_dve(S_LOOP)
            side_dve(S_LOOP + 1)
            dve.wait_ge(late_in, 48)
            dve.wait_ge(s_w, 1)
            dve.tensor_scalar(nkk[:], kkey[:, :, SEQ:T], -1.0, None, ALU.mult)
            dve.drain()
            dve.sem_inc(s_nk, 1)
            for j in range(PAIRS):
                s_j = sst[:, j]
                dve.wait_ge(s_pe, 2 * j + 1)
                dve.tensor_tensor(s_j, s_j, bcast(wdec[:, j], HD), ALU.mult)
                u_, v_ = (A4[2 * (j % 2) + q][:].rearrange("p (b n) -> p b n", n=HD) for q in range(2))
                dve.tensor_tensor(st[:], u_, bcast(iclr[:, j, SEQ:T], HD), ALU.mult)
                dve.drain()
                dve.tensor_tensor(s_j, s_j, st[:], ALU.add)
                dve.drain()
                dve.tensor_tensor(st[:], v_, bcast(K_[:, j, SEQ:T], HD), ALU.mult)
                dve.drain()
                dve.tensor_tensor(s_j, s_j, st[:], ALU.add).then_inc(s_vec, 1)
                dve.drain()
            dve.wait_ge(s_pe, 2 * PAIRS + 1)
            dve.tensor_copy(kkey[:, :, SEQ:T], A4[0][:, 0:PAIRS * DEC].rearrange("p (j b) -> p j b", b=DEC))
            dve.drain()
            dve.sem_inc(s_y, 1)
            side_dve(S_LOOP + 2)
            for n in range(RT):
                dve.wait_ge(n_pe, n + 1)
                dve.tensor_tensor(kkey[:, n], kkey[:, n], A4[n % 4][:, 0:T], ALU.subtract).then_inc(n_vec, 1)
            side_dve(S_LOOP + 3)
            dve.wait_ge(n_act, 2 * RT)
            dve.reciprocal(gn[:], gn[:])
            dve.drain()
            dve.tensor_tensor(kkey[:], kkey[:], gn[:], ALU.mult)
            dve.drain()
            dve.tensor_tensor(gn[:], R_, K_, ALU.mult)
            dve.tensor_tensor(kkey[:], kkey[:], bcast(pp("lnw"), T), ALU.mult)
            dve.drain()
            dve.tensor_tensor(gn[:], gn[:], bcast(pp("rk"), T), ALU.mult)
            dve.tensor_tensor(kkey[:], kkey[:], bcast(pp("lnb"), T), ALU.add)
            dve.drain()
            dve.sem_inc(n_bonus, 1)
            side_dve(S_LOOP + 4)
            for n in range(RT):
                dve.wait_ge(n_pe, 2 * RT + n + 1)
                dve.tensor_tensor(gn[:, n], V_[:, n], A4[n % 4][:, 0:T], ALU.mult).then_inc(n_vec, 1)
            dve.drain()
            dve.tensor_tensor(kkey[:], kkey[:], gn[:], ALU.add)
            dve.drain()
            side_dve(S_LOOP + 5)
            for n in range(RT):
                dve.wait_ge(n_pe, 3 * RT + n + 1)
                dve.tensor_tensor(kkey[:, n], kkey[:, n], A4[n % 4][:, 0:T], ALU.mult).then_inc(n_vec, 1)
            dve.drain()
            dve.wait_ge(n_pe, 4 * RT)
            dve.wait_ge(mixst, 48)
            dve.tensor_copy(oah[:], kkey[:])
            dve.drain()
            dve.tensor_tensor(oal[:], kkey[:], oah[:].bitcast(F32), ALU.subtract)
            dve.drain()
            dve.sem_inc(oa_done, 1)
            side_dve(S_LOOP + 6)
            side_dve(S_LOOP + 7)
            dve.wait_ge(a_act, 1 + 2 * AT)
            dve.reciprocal(qn2[:], qn2[:])
            dve.drain()
            for s, gain in ((0, "qn"), (1, "kn")):
                t = slice(s * AT, s * AT + AT)
                dve.scalar_tensor_tensor(qkv[:, t], qkv[:, t], pp(gain), qn2[:, t], ALU.mult, ALU.mult)
            dve.drain()
            dve.sem_inc(a_vec, 1)
            side_dve(S_LOOP + 8)
            for n in range(2 * AT):
                dve.wait_ge(a_pe, 2 * AT + n + 1)
                dve.tensor_tensor(qn2[:, n], cossin[:, 1], A4[n % 4][:, 0:T], ALU.mult).then_inc(a_sin, 1)
            dve.sem_inc(a_vec, 1)
            dve.tensor_tensor(qkv[:, 0:2 * AT], qkv[:, 0:2 * AT], over(cossin[:, 0], 2 * AT), ALU.mult)
            dve.drain()
            dve.tensor_tensor(qkv[:, 0:2 * AT], qkv[:, 0:2 * AT], qn2[:], ALU.add)
            dve.drain()
            dve.sem_inc(a_vec, 1)
            side_dve(S_LOOP + 9)
            dve.wait_ge(amask_in, 16)
            for hh in range(HPG):
                dve.wait_ge(t_pe, 1 + 4 * hh + 1)
                dve.scalar_tensor_tensor(sc[:, :, 0:P], A4[0][:, 0:3 * P].rearrange("p (g n) -> p g n", g=3), SCALE,
                                         amask[:, :, 0:P], ALU.mult, ALU.add)
                dve.scalar_tensor_tensor(sc[:, 0:2, P:], A4[1][:].rearrange("p (g n) -> p g n", g=2), SCALE,
                                         amask[:, 0:2, P:], ALU.mult, ALU.add)
                dve.scalar_tensor_tensor(sc[:, 2, P:], A4[2][:, 0:SEQ], SCALE, amask[:, 2, P:], ALU.mult, ALU.add)
                dve.drain()
                dve.sem_inc(t_vec, 1)
                dve.tensor_reduce(mx[:, 0:1], sc[:, :, 0:P], AX.XY, ALU.max)
                dve.tensor_reduce(mx[:, 1:2], sc[:, :, P:], AX.XY, ALU.max)
                dve.drain()
                dve.tensor_scalar(nmx[:], mx[:], -1.0, None, ALU.mult)
                dve.drain()
                dve.sem_inc(t_vec, 1)
                if hh < 2:
                    side_dve(S_LOOP + 10 + hh)
                dve.wait_ge(t_act, 1 + 3 * hh + 1)
                dve.reciprocal(rl[:], ls[:])
                dve.drain()
                dve.tensor_scalar(sc[:, :, 0:P], sc[:, :, 0:P], rl[:, 0:1], None, ALU.mult)
                dve.tensor_scalar(sc[:, :, P:], sc[:, :, P:], rl[:, 1:2], None, ALU.mult)
                dve.drain()
                dve.sem_inc(t_vec, 2)
                dve.wait_ge(t_pe, 1 + 4 * hh + 2)
            dve.wait_ge(t_act, 1 + 3 * HPG)
            dve.tensor_tensor(pnew[:], qkv[:, 0:AT, SEQ:T], qkv[:, AT:2 * AT, SEQ:T], ALU.mult).then_inc(u_vec, 1)
            dve.wait_ge(u_act, 3)
            dve.tensor_reduce(smx[:], ss[:], AX.X, ALU.max)
            dve.drain()
            wide = smx[:].unsqueeze(2).to_broadcast([DEC, HPG, NKEYS + 3])
            dve.tensor_tensor(ss[:], ss[:], wide, ALU.subtract).then_inc(u_vec, 1)
            dve.wait_ge(u_act, 4)
            dve.drain()
            dve.tensor_reduce(smx[:], ss[:], AX.X, ALU.add)
            dve.drain()
            dve.reciprocal(smx[:], smx[:])
            dve.drain()
            dve.tensor_tensor(ss[:], ss[:], wide, ALU.mult).then_inc(u_vec, 1)
            dve.wait_ge(u_act, 5)
            dve.wait_ge(u_pe, 5)
            dve.tensor_tensor(pnew[:], pnew[:], qkv[:, 2 * AT:3 * AT, SEQ:T], ALU.mult)
            dve.drain()
            dve.tensor_tensor(ob[:, :, SEQ:T], pnew[:], A4[0][:, 0:AT * DEC].rearrange("p (t b) -> p t b", b=DEC), ALU.add)
            dve.drain()
            dve.tensor_copy(obh[:], ob[:])
            dve.drain()
            dve.tensor_tensor(obl[:], ob[:], obh[:].bitcast(F32), ALU.subtract)
            dve.wait_ge(mixst, 16 * 7)
            dve.drain()
            dve.sem_inc(ob_done, 1)

            def merge(n, i):
                ahead("branch", n, i, split_lo)
                block_done(dve, "branch", n, i)
                m = n + BODY * i
                dve.wait_ge(gate_done, 2 * n + 2 + 2 * BODY * i)
                dve.tensor_tensor(mg[:, 0], gates[:, m], result("branch", n)[:, 0:T], ALU.mult)
                dve.tensor_tensor(mg[:, 1], gates[:, DT + m], A4[n % 4][:, 0:T], ALU.mult)
                dve.drain()
                dve.sem_inc(evac, 1)
                dve.tensor_tensor(mg[:, 0], mg[:, 0], mg[:, 1], ALU.add)
                dve.drain()
                dve.tensor_copy(hhi[:, m], mg[:, 0])
                dve.drain()
                dve.tensor_tensor(hlo[:, m], mg[:, 0], hhi[:, m].bitcast(F32), ALU.subtract).then_inc(m_done, 1)
                dve.drain()
            walk(dve, "branch", merge)

            def add(n, i):
                ahead("out", n, i, split_lo)
                block_done(dve, "out", n, i)
                m = n + BODY * i
                dve.tensor_tensor(x[:, m], x[:, m], result("out", n)[:, 0:T], ALU.add).then_inc(evac, 1)
            walk(dve, "out", add)

        def stream(name, hi, lo, before=None):
            walk(pe, name, lambda n, i: products(name, n, i, [(result(name, n), KT_OF[FIRST[name]], hi, lo)],
                                                 before if n == 0 else None))

        def per_head(bank, width, col0, *terms):
            for j, p in each_head():
                out = bank(j)[half(p), col0(j):col0(j) + width]
                for t, (lhs, rhs) in enumerate(terms):
                    mm = pe.matmul(out, lhs(j, p), rhs(j, p), start=(t == 0), stop=(t == len(terms) - 1))
            return mm

        def part(buf, lo=0, n=C):
            return lambda j, p: buf[half(p), j, lo:lo + n]

        def ident(j, p):
            return cc("ident64")[half(p)]

        def mix_pe():
            def h_there(k):
                if k % 4 == 0:
                    pe.wait_ge(h_done, DT + k + 4)
            stream("lora", hhi, hlo, h_there)
            pe.wait_ge(mix_in, 64)
            pe.wait_ge(lora_act, 1)
            for n in range(2 * RT):
                if n >= 4:
                    pe.wait_ge(lora_out, n - 3)
                p = n % 2
                pe.matmul(A4[n % 4][:, 0:T], w2a2[half(p), n // 2 * P:n // 2 * P + P], lora[half(p), 0],
                          start=True, stop=True).then_inc(lora_pe, 1)
            stream("rkv", hhi, hlo)
            side_pe(0)
            side_pe(1)
            pe.wait_ge(kk_sq, 1)
            pe.wait_ge(lora_out, 2 * RT)
            for n in range(RT):
                if n >= 4:
                    pe.wait_ge(kk_root, n - 3)
                pe.matmul(A4[n % 4][:, 0:T], cc("blocks"), nrm[:, n], start=True, stop=True).then_inc(kk_ss, 1)
            for n in range(2, S_PREP):
                side_pe(n)
            pe.wait_ge(prep, 1)
            one = lambda b: (lambda j: A4[b])
            two = lambda b: (lambda j: A4[b + j // 4])
            c64 = lambda j: C * j
            with pe.Fori(0, NCH) as c:
                extra = lambda k, halves=(0, 1): side_pe(S_PREP + k, S_CHUNK // BODY * c, halves)
                pe.wait_ge(c_free, c + 1)
                pe.wait_ge(c_vec, 3 * c + 1)
                pe.sem_inc(passed, 1)
                per_head(two(0), 2 * C, lambda j: 2 * C * (j % 4), (part(bc), part(ar, 0, 2 * C))).then_inc(c_pe, 1)
                per_head(two(2), 2 * C, lambda j: 2 * C * (j % 4), (part(kc), part(ar, 0, 2 * C))).then_inc(c_pe, 1)
                extra(0)
                pe.wait_ge(c_op, c + 1)
                pe.wait_ge(c_vec, 3 * c + 2)
                pe.sem_inc(passed, 1)
                per_head(one(0), C, c64, (part(ar), part(bc)))
                per_head(one(1), C, c64, (part(vc), ident))
                pe.wait_ge(c_vec, 3 * c + 3)
                pe.sem_inc(passed, 1)
                per_head(one(2), C, c64, (part(bc), ident))
                per_head(one(3), C, c64, (part(kc), ident)).then_inc(c_pe, 1)
                extra(1)
                for lv in range(1, 6):
                    pe.wait_ge(c_lv, 6 * c + lv)
                    pe.sem_inc(passed, 1)
                    if lv == 1:
                        pe.wait_ge(c_act, 10 * c + 3)
                    pe.sem_inc(passed, 1)
                    per_head(one(0), C, c64, (part(zm), part(tm))).then_inc(c_m1, 1)
                    extra(1 + lv, (0,))
                    pe.wait_ge(c_act, 10 * c + 3 + lv)
                    pe.sem_inc(passed, 1)
                    mm = per_head(one(1), C, c64, (part(m1), part(qm)))
                    if lv < 5:
                        mm = per_head(one(2), C, c64, (part(qm), part(m1)))
                    mm.then_inc(c_pe, 1)
                    extra(1 + lv, (1,))
                per_head(one(3), C, c64, (part(ar), part(state)), (part(ak), part(vt))).then_inc(c_w1, 1)
                extra(7, (0,))
                pe.wait_ge(c_act, 10 * c + 9)
                pe.wait_ge(c_lv, 6 * c + 6)
                pe.sem_inc(passed, 1)
                per_head(one(0), C, c64, (part(qm), part(w1))).then_inc(c_w1, 1)
                extra(7, (1,))
                pe.wait_ge(c_act, 10 * c + 10)
                pe.sem_inc(passed, 1)
                per_head(one(1), C, c64, (part(state), part(ar, C)), (part(um), part(ab, C)), (part(vt), part(ak, C)))
                per_head(one(2), C, c64, (part(bt), part(um)), (part(kt_), part(vt))).then_inc(c_pe, 1)
            side_pe(S_LOOP)
            side_pe(S_LOOP + 1)
            pe.wait_ge(c_free, 1 + NCH)
            pe.wait_ge(late_in, 48)
            pe.wait_ge(s_nk, 1)
            for j in range(PAIRS):
                if j >= 2:
                    pe.wait_ge(s_vec, j - 1)
                for p in range(2):
                    for b in range(DEC):
                        out = slice(b * HD, b * HD + HD)
                        pe.matmul(A4[2 * (j % 2)][half(p), out], nkk[half(p), j, b:b + 1].to_broadcast([HD, HD]),
                                  sst[half(p), j, b], start=True, stop=True)
                        mm = pe.matmul(A4[2 * (j % 2) + 1][half(p), out],
                                       V_[half(p), j, SEQ + b:SEQ + b + 1].to_broadcast([HD, HD]), ident(j, p),
                                       start=True, stop=True)
                mm.then_inc(s_pe, 2)
            pe.wait_ge(s_vec, PAIRS)
            for j, p in each_head():
                for b in range(DEC):
                    mm = pe.matmul(A4[0][half(p), j * DEC + b:j * DEC + b + 1], sst[half(p), j, b],
                                   R_[half(p), j, SEQ + b:SEQ + b + 1], start=True, stop=True)
            mm.then_inc(s_pe, 1)
            side_pe(S_LOOP + 2)
            pe.wait_ge(s_y, 1)
            for n in range(RT):
                if n >= 4:
                    pe.wait_ge(n_vec, n - 3)
                pe.matmul(A4[n % 4][:, 0:T], cc("blocks64"), kkey[:, n], start=True, stop=True).then_inc(n_pe, 1)
            side_pe(S_LOOP + 3)
            for n in range(RT):
                pe.wait_ge(n_act, n + 1 if n < 4 else RT + n - 3)
                if n < 4:
                    pe.wait_ge(n_vec, 4 + n + 1)
                pe.matmul(A4[n % 4][:, 0:T], cc("blocks64"), gn[:, n], start=True, stop=True).then_inc(n_pe, 1)
            side_pe(S_LOOP + 4)
            pe.wait_ge(n_bonus, 1)
            for n in range(RT):
                if n >= 4:
                    pe.wait_ge(n_vec, RT + n - 3)
                pe.matmul(A4[n % 4][:, 0:T], cc("blocks"), gn[:, n], start=True, stop=True).then_inc(n_pe, 1)
            side_pe(S_LOOP + 5)
            for n in range(RT):
                pe.wait_ge(n_vec, 2 * RT + n - 3)
                col = slice(n * P, n * P + P)
                pe.matmul(A4[n % 4][:, 0:T], g2a[:, col], lora[:, 1], start=True, stop=False)
                pe.matmul(A4[n % 4][:, 0:T], g2b[96:P, col], lora[96:P, 2], start=False, stop=True).then_inc(n_pe, 1)
            side_pe(S_LOOP + 6)
            side_pe(S_LOOP + 7)
            pe.wait_ge(oa_done, 1)
            pe.wait_ge(a_act, 1)
            for n in range(2 * AT):
                if n >= 4:
                    pe.wait_ge(a_act, n - 2)
                pe.matmul(A4[n % 4][:, 0:T], cc("blocks"), qn2[:, n], start=True, stop=True).then_inc(a_pe, 1)
            side_pe(S_LOOP + 8)
            pe.wait_ge(a_vec, 1)
            for n in range(2 * AT):
                if n >= 4:
                    pe.wait_ge(a_sin, n - 3)
                pe.matmul(A4[n % 4][:, 0:T], cc("rot"), qkv[:, n], start=True, stop=True).then_inc(a_pe, 1)
            pe.wait_ge(a_sin, 2 * AT)
            for q in range(2):
                for t in range(AT):
                    bank, col = divmod(t * P, 512)
                    mm = pe.transpose(A4[2 * q + bank][:, col:col + P], qkv[:, 2 * AT + t, q * P:q * P + P], cc("ident"))
            mm.then_inc(t_pe, 1)
            side_pe(S_LOOP + 9)
            pe.wait_ge(a_vec, 3)
            pe.wait_ge(t_act, 1)
            for hh in range(HPG):
                if hh:
                    pe.wait_ge(t_act, 1 + 3 * hh)
                heads = [divmod(g * HPG + hh, 2) for g in range(3)]
                for g, (j, p) in enumerate(heads):
                    pe.matmul(A4[0][:, g * P:g * P + P], qkv[half(p), j, 0:P], qkv[half(p), AT + j, 0:P],
                              start=True, stop=True)
                for g, (j, p) in enumerate(heads):
                    mm = pe.matmul(A4[1 + g // 2][:, g % 2 * SEQ:g % 2 * SEQ + SEQ], qkv[half(p), j, P:SEQ],
                                   qkv[half(p), AT + j, 0:SEQ], start=True, stop=True)
                mm.then_inc(t_pe, 1)
                if hh < 2:
                    side_pe(S_LOOP + 10 + hh)
                pe.wait_ge(t_vec, 4 * hh + 4)
                for g in range(3):
                    for c in range(3):
                        mm = pe.transpose(A4[g][:, c * P:c * P + P], sc[:, g, c * P:c * P + P], cc("ident"))
                mm.then_inc(t_pe, 1)
                pe.wait_ge(t_act, 1 + 3 * hh + 2)
                for g, (j, p) in enumerate(heads):
                    bank, col = ((3, 0), (3, SEQ), (0, 0))[g]
                    v = slice(j * P + HD * p, j * P + HD * p + HD)
                    pe.matmul(A4[bank][half(p), col:col + P], vtok[:, 0, v], pt[:, g, 0:P], start=True, stop=True)
                    later = A4[bank][half(p), col + P:col + SEQ]
                    pe.matmul(later, vtok[:, 0, v], pt[:, g, P:SEQ], start=True, stop=False)
                    mm = pe.matmul(later, vtok[:, 1, v], pt[:, g, SEQ:], start=False, stop=True)
                mm.then_inc(t_pe, 2)
            pe.wait_ge(t_act, 1 + 3 * HPG)
            for t in range(2 * AT):
                mm = pe.transpose(A4[t // 4][0:DEC, t % 4 * P:t % 4 * P + P], qkv[:, AT + t, SEQ:T], cc("ident"))
            mm.then_inc(u_pe, 1)
            pe.wait_ge(cache_in, 64)
            pe.wait_ge(u_act, 1)
            for h in range(A_HEADS):
                (j, p), (g, hh) = divmod(h, 2), divmod(h, HPG)
                koff = 2 * KOFF[g] + (j % 2) * KEYS[g]
                for b in range(DEC):
                    col = g * 32 + hh * DEC + b
                    mm = pe.matmul(A4[3 - p][0:KEYS[g], col:col + 1], kca[half(p), b, koff:koff + KEYS[g]],
                                   qkv[half(p), j, SEQ + b:SEQ + b + 1], start=True, stop=True)
            mm.then_inc(u_pe, 1)
            pe.wait_ge(u_vec, 1)
            pe.wait_ge(u_act, 2)
            for t in range(AT):
                pe.matmul(A4[0][0:DEC, 2 * t:2 * t + 2], pnew[:, t], cc("pairsum"), start=True, stop=True)
            for hh in range(HPG):
                for g in range(3):
                    col = hh % 2 * NKEYS + KOFF[g]
                    mm = pe.transpose(A4[1 + hh // 2][0:DEC, col:col + KEYS[g]], sct[0:KEYS[g], g, hh],
                                      cc("ident")[0:KEYS[g], 0:KEYS[g]])
            mm.then_inc(u_pe, 1)
            pe.wait_ge(u_vec, 3)
            for hh in range(HPG):
                for g in range(3):
                    col = g * 32 + hh * DEC
                    pe.transpose(A4[3][0:KEYS[g], col:col + DEC], ss[:, hh, KOFF[g]:KOFF[g] + KEYS[g]],
                                 cc("ident")[0:DEC, 0:DEC])
            for t in range(AT):
                g, h0 = t // 2, 2 * (t % 2)
                for p in range(2):
                    mm = pe.matmul(A4[1][half(p), t * DEC:t * DEC + DEC],
                                   ss[:, h0 + p, NKEYS + g:NKEYS + g + 1].to_broadcast([DEC, HD]),
                                   cc("ident")[0:DEC, 0:DEC], start=True, stop=True)
            mm.then_inc(u_pe, 1)
            pe.wait_ge(u_act, 5)
            for h in range(A_HEADS):
                (j, p), (g, hh) = divmod(h, 2), divmod(h, HPG)
                nk = KEYS[g]
                for b in range(DEC):
                    mm = pe.matmul(A4[0][half(p), j * DEC + b:j * DEC + b + 1],
                                   vca[0:nk, b // 4, b % 4, g, hh * HD:hh * HD + HD], pts[0:nk, g, hh, b:b + 1],
                                   start=True, stop=True)
            mm.then_inc(u_pe, 1)
            pe.wait_ge(ob_done, 1)
            walk(pe, "branch", lambda n, i: products(
                "branch", n, i, [(result("branch", n), RT, oah, oal), (A4[n % 4], AT, obh, obl)]))

            def merged(k):
                if k == 0 or k >= DT - 2:
                    pe.wait_ge(m_done, max(k + 1, DT - 2))
            stream("out", hhi, hlo, merged)

        passed, c_m1, c_w1, c_lv, s_nk, s_y, n_bonus, a_sin = map(
            sem, ("passed", "c_m1", "c_w1", "c_lv", "s_nk", "s_y", "n_bonus", "a_sin"))

        block = ctx.enter_context(nc.Block())

        @block.sync
        def _(sp):
            sp.dma_start(ones[:], ins["ones"]).then_inc(loaded, 16)
            for q in range(4):
                sp.dma_start(x[:, 4 * q:4 * q + 4], ins["x"][:, 4 * q:4 * q + 4]).then_inc(x_in[q], 16)
            sp.dma_start(xin_gains[:], ins["gains"]).then_inc(loaded, 16)
            for name, n, kt in PHASES:
                b0 = FIRST[name]
                at = OFFSET[b0] * P * P
                cols = kt // 2 * P
                src = w[at:at + n * P * kt * P].rearrange("(u p n) -> u p n", p=P, n=cols)

                def load(k, i):
                    u = 2 * b0 + k
                    if u >= RING or not isinstance(i, int):
                        sp.wait_ge(lo_done, u - RING + 1 + RING * i)
                    sp.dma_start(raw[:, u % RING, 0:cols], src[k + RING * i]).then_inc(landed[u % RING], 16)
                first = RING if b0 == 0 else 0
                for k in range(first):
                    load(k, 0)
                loops = (2 * n - first) // RING
                if loops:
                    with sp.Fori(0, loops) as i:
                        for k in range(RING):
                            load(first + k, i)
                for k in range(first + RING * loops, 2 * n):
                    load(k, 0)
            sp.wait_ge(evac, BANKS + NBLK)
            sp.dma_start(outs["y"], x[:]).then_inc(stored, 16)
            sp.wait_ge(stored, 16)

        @block.scalar
        def _(_act):
            norm_act(0)
            for u in range(1, LOOK):
                split_hi(u, 0, HALF)
            ffn_act(1)
            norm_act(1)
            mix_act()
            norm_act(2)
            ffn_act(2)

        @block.vector
        def _(_dve):
            dve.memset(eps[:, 0:1], EPS)
            dve.memset(eps[:, 1:2], LN_EPS).then_inc(evac, BANKS)
            split_lo(0, 0, HALF)
            norm_dve(0)
            for u in range(1, LOOK):
                split_lo(u, 0, HALF)
            ffn_dve(1)
            norm_dve(1)
            mix_dve()
            norm_dve(2)
            ffn_dve(2)

        @block.tensor
        def _(_pe):
            pe.wait_ge(loaded, LOADED)
            pe.sem_inc(half_done, 1)
            norm_pe(0)
            ffn_pe(1, 0)
            norm_pe(1)
            mix_pe()
            norm_pe(2)
            ffn_pe(2, 2)

        @block.gpsimd
        def _(gp):
            mix_pool(gp)


def tiles_of(w, cols, rows=None):
    w = w if rows is None else w[rows]
    k = w.shape[0] // P
    return np.stack([w[:, c:c + P].reshape(2, k // 2, P, P).transpose(0, 2, 1, 3).reshape(2, P, k // 2 * P)
                     for c in cols])


def ffn_blocks(w_in, w_out):
    out, f0 = [], 0
    for kt in FFN_PARTS:
        cols = [c for j in range(kt) for c in ((f0 + j) * P, D_FF + (f0 + j) * P)]
        out.append(tiles_of(w_in, cols))
        out.append(tiles_of(w_out, range(0, D, P), slice(f0 * P, (f0 + kt) * P)))
        f0 += kt
    return out


def feature_major(a):
    return np.ascontiguousarray(a.T.reshape(-1, P, a.shape[0]).transpose(1, 0, 2))


def rwkv_cols(a):
    a = np.concatenate([a[:, :LORA0 + 2 * P], a[:, G_LAST:]], 1)
    return feature_major(a)


def kernel(**inputs):
    import concourse.bacc as bacc
    from concourse.bass_utils import run_bass_kernel_spmd

    g = {k: np.asarray(v) for k, v in inputs.items()}
    l0 = {k: v[0] for k, v in g.items() if not k.startswith("x_")}
    w_in, at0, ga0 = l0["w_in"], N_RW, N_RW + 3 * D_AT
    blocks = ffn_blocks(l0["ffn1_w_in"], l0["ffn1_w_out"])
    blocks += [tiles_of(w_in, (LORA0, LORA0 + P, G_LAST)), tiles_of(w_in, range(0, 3 * D_RW, P)),
               tiles_of(w_in, range(at0, ga0 + 2 * D, P)),
               tiles_of(np.concatenate([l0["w_branch_rwkv"], l0["w_branch_attn"]]), range(0, D, P)),
               tiles_of(l0["w_out"], range(0, D, P))]
    blocks += ffn_blocks(l0["ffn2_w_in"], l0["ffn2_w_out"])
    par = [rwkv_cols(l0["rwkv_mu"][None])[:, :, 0]]
    par += [l0[k].reshape(-1, P).T for k in ("rwkv_w0", "rwkv_a0", "rwkv_k_k", "rwkv_k_a", "rwkv_r_k", "rwkv_ln_w",
                                             "rwkv_ln_b", "b_gate")]
    par += [np.tile(l0[k], 2)[:, None] for k in ("attn_q_norm", "attn_k_norm")]
    caches = [l0[f"cache_att_w{w}"] for w, _ in GROUPS]
    seen = [c[:, ::step][:, :n] for c, (_, step), n in zip(caches, GROUPS, KEYS)]
    kcache = np.concatenate([c[:, :, 0].reshape(DEC, n, 2, P).transpose(3, 0, 2, 1).reshape(P, DEC, 2 * n)
                             for c, n in zip(seen, KEYS)], 2)
    g2b = np.zeros((P, D_RW), np.float32)
    g2b[96:] = l0["rwkv_g2"][P:]
    arrays = {
        "weights": np.concatenate([b.reshape(-1) for b in blocks]),
        "x": feature_major(np.concatenate([g["x_prompt"][0], g["x_sample"][:, 0]])),
        "gains": np.ascontiguousarray(np.stack([l0[k].reshape(DT, P).T for k in ("ffn1_norm", "mix_norm", "ffn2_norm")], 1)),
        "ones": np.ones((P, P), np.float32),
        "consts": np.concatenate(list(CONST.values()), 1),
        "params": np.concatenate(par, 1),
        "shift": rwkv_cols(l0["state_rwkv_shift"]),
        "w2a2": np.concatenate([l0["rwkv_w2"], l0["rwkv_a2"]]),
        "g2a": np.ascontiguousarray(l0["rwkv_g2"][:P]),
        "g2b": g2b,
        "swkv": np.ascontiguousarray(l0["state_rwkv_wkv"].reshape(DEC, PAIRS, 2, HD, HD).transpose(2, 4, 1, 0, 3)
                                     .reshape(P, PAIRS, DEC, HD)),
        "kcache": np.ascontiguousarray(kcache),
    }
    for i, (c, s, n) in enumerate(zip(caches, seen, KEYS)):
        arrays[f"cache{i}"] = c.reshape(DEC, c.shape[1], 2 * HPG * HD)
        arrays[f"vcache{i}"] = np.ascontiguousarray(s[:, :, 1].reshape(2, DEC // 2, n, HPG * HD).transpose(2, 0, 1, 3))
    shapes = {"y": (P, DT, T), "last": (P, 3 * RT + 3, DEC + 1), "pwkv": (P, PAIRS, HD),
              "swkv": (P, PAIRS, DEC, HD), "pkv": (P, 2 * AT, SEQ)}
    shapes.update({f"skv{i}": (DEC, n, 2 * HPG * HD) for i, n in enumerate(KOUT)})
    nc = bacc.Bacc("TRN2", target_bir_lowering=False, num_devices=1)
    ins = {k: nc.dram_tensor(f"in_{k}", a.shape, F32, kind="ExternalInput").ap() for k, a in arrays.items()}
    outs = {k: nc.dram_tensor(f"out_{k}", s, F32, kind="ExternalOutput").ap() for k, s in shapes.items()}
    side = nc.dram_tensor("side", (3 * AT + 2 * DT, P, T), F32, kind="Internal").ap()
    build(nc, ins, outs, side)
    r = run_bass_kernel_spmd(nc, [{f"in_{k}": a for k, a in arrays.items()}], core_ids=[0]).results[0]
    y = r["out_y"].transpose(2, 1, 0).reshape(T, D)
    last = r["out_last"].transpose(2, 1, 0).reshape(DEC + 1, -1)
    last = np.concatenate([last[:, :LORA0 + 2 * P], last[:, -(N_RW - LORA0 - 2 * P):]], 1)
    pwkv = r["out_pwkv"].reshape(2, HD, PAIRS, HD).transpose(2, 0, 3, 1).reshape(1, 1, HEADS, HD, HD)
    swkv = r["out_swkv"].reshape(2, HD, PAIRS, DEC, HD).transpose(3, 2, 0, 4, 1).reshape(1, DEC, HEADS, HD, HD)
    pkv = r["out_pkv"].transpose(2, 1, 0).reshape(SEQ, 2, 3, HPG, HD)
    prompt = [pkv[None, None, SEQ - min(w, SEQ):, :, i] for i, (w, _) in enumerate(GROUPS)]
    sample = [r[f"out_skv{i}"].reshape(1, DEC, n, 2, HPG, HD) for i, n in enumerate(KOUT)]
    out = (y[None, :SEQ], y[SEQ:, None], last[None, :1], pwkv, *prompt, last[None, 1:], swkv, *sample)
    return tuple(np.ascontiguousarray(a) for a in out)
```
